# Optimizing a Trainium2 kernel written in Bass

```python
import math
import jax, jax.numpy as jnp
from jax import lax
import numpy as np

D_MODEL = 1024
BATCH = 1
SEQ = 1024
DEPTH = 1

HEAD_DIM = 64
A_HEADS = 8
A_KV = 2
A_REP = A_HEADS // A_KV
A_WINDOW = 128
A_BLOCK = 128
B_HEADS = 8
B_KV = 2
B_REP = B_HEADS // B_KV
CMP_LEN = 32
CMP_STRIDE = 16
CMP_HIDDEN = 256
SEL_BLOCK = 64
SEL_TOPN = 16
SEL_Q_CHUNK = 64
B_WINDOW = 512
B_WIN_BLOCK = 128
N_BUCKETS = 32
MAX_EXACT = 16
MAX_DIST = 128
TOTAL_HEADS = A_HEADS + B_HEADS
N_GROUPS = 4
EXPERTS_PER_GROUP = 8
N_EXPERTS = N_GROUPS * EXPERTS_PER_GROUP
TOP_K_IN_GROUP = 2
EXPERT_FF = 512
MOE_BLOCK = 128

RMS_EPS = 1e-5
NEG = -1e30
FORCE = 1e9

A_QW = A_HEADS * HEAD_DIM
A_KVW = A_KV * HEAD_DIM
B_QW = B_HEADS * HEAD_DIM
B_KVW = B_KV * HEAD_DIM
IN_SIZES = (A_QW, A_KVW, A_KVW, B_QW, B_KVW, B_KVW, B_KVW, B_KVW, B_KVW, B_KVW, 3 * B_HEADS, 2 * D_MODEL)
IN_COLS = sum(IN_SIZES)

kernel_name = "hybrid_swa_sink_nsa_hier_moe"

def rmsnorm(x, g):
    xf = x.astype(jnp.float32)
    y = xf * lax.rsqrt(jnp.mean(xf * xf, axis=-1, keepdims=True) + RMS_EPS)
    return y.astype(x.dtype) * g

def t5_bucket(dist):
    n = jnp.maximum(dist, 0)
    nf = jnp.maximum(n, 1).astype(jnp.float32)
    large = MAX_EXACT + (jnp.log(nf / MAX_EXACT) / math.log(MAX_DIST / MAX_EXACT)
                         * (N_BUCKETS - MAX_EXACT)).astype(jnp.int32)
    large = jnp.minimum(large, N_BUCKETS - 1)
    return jnp.where(n < MAX_EXACT, n, large)

def softmax_with_sink(s, sink):
    sink = sink.astype(jnp.float32)
    m = jnp.maximum(jnp.max(s, axis=-1, keepdims=True), sink)
    e = jnp.exp(s - m)
    return e / (jnp.sum(e, axis=-1, keepdims=True) + jnp.exp(sink - m))

def banded_attention(q, k, v, window, block, bias_tab, sinks):
    B, S, G, R, Dh = q.shape
    nb = S // block
    npv = -(-(window - 1) // block)
    L = (npv + 1) * block
    qb = q.reshape(B, nb, block, G, R, Dh)
    pad = ((0, 0), (npv * block, 0), (0, 0), (0, 0))
    kp = jnp.pad(k, pad)
    vp = jnp.pad(v, pad)
    kidx = jnp.arange(nb)[:, None] * block + jnp.arange(L)[None, :]
    kb = kp[:, kidx]
    vb = vp[:, kidx]
    qpos = jnp.arange(nb)[:, None] * block + jnp.arange(block)[None, :]
    kpos = kidx - npv * block
    dist = qpos[:, :, None] - kpos[:, None, :]
    valid = (dist >= 0) & (dist < window) & (kpos[:, None, :] >= 0)
    bias = bias_tab[t5_bucket(dist)].reshape(nb, block, L, G, R)
    bias = jnp.transpose(bias, (3, 4, 0, 1, 2)).astype(jnp.float32)
    s = jnp.einsum('bnqgrd,bnkgd->bgrnqk', qb, kb).astype(jnp.float32) * (Dh ** -0.5) + bias
    s = jnp.where(valid, s, NEG)
    if sinks is None:
        p = jax.nn.softmax(s, axis=-1)
    else:
        p = softmax_with_sink(s, sinks.reshape(G, R, 1, 1, 1))
    o = jnp.einsum('bgrnqk,bnkgd->bnqgrd', p.astype(v.dtype), vb)
    return o.reshape(B, S, G * R * Dh)

def nsa_compressed_selected(q, kc, vc, ks, vs, pos_k, w1_k, w2_k, pos_v, w1_v, w2_v, bias_tab):
    B, S, G, R, Dh = q.shape
    nc = (S - CMP_LEN) // CMP_STRIDE + 1
    ns = S // SEL_BLOCK
    n_sel = min(SEL_TOPN, ns)
    cidx = jnp.arange(nc)[:, None] * CMP_STRIDE + jnp.arange(CMP_LEN)[None, :]

    def compress(t, pos, w1, w2):
        blocks = t[:, cidx] + pos[:, None, :]
        blocks = jnp.transpose(blocks, (0, 3, 1, 2, 4)).reshape(B, G, nc, CMP_LEN * Dh)
        return jax.nn.gelu(blocks @ w1) @ w2

    kcmp = compress(kc, pos_k, w1_k, w2_k)
    vcmp = compress(vc, pos_v, w1_v, w2_v)
    cstart = jnp.arange(nc) * CMP_STRIDE
    cend = cstart + CMP_LEN - 1
    sstart = jnp.arange(ns) * SEL_BLOCK
    overlap = ((cstart[:, None] < sstart[None, :] + SEL_BLOCK)
               & (cstart[:, None] + CMP_LEN > sstart[None, :])).astype(jnp.float32)
    ksb = jnp.transpose(ks.reshape(B, ns, SEL_BLOCK, G, Dh), (0, 3, 1, 2, 4))
    vsb = jnp.transpose(vs.reshape(B, ns, SEL_BLOCK, G, Dh), (0, 3, 1, 2, 4))
    tab = jnp.transpose(bias_tab.reshape(N_BUCKETS, G, R), (1, 0, 2))
    nq = S // SEL_Q_CHUNK
    qch = jnp.moveaxis(q.reshape(B, nq, SEL_Q_CHUNK, G, R, Dh), 1, 0)
    bi = jnp.arange(B)[:, None, None, None]
    gi = jnp.arange(G)[None, :, None, None]
    scale = Dh ** -0.5
    jsel = jnp.arange(ns)

    def chunk(args):
        qc, c = args
        t = c * SEL_Q_CHUNK + jnp.arange(SEL_Q_CHUNK)
        sc = jnp.einsum('bqgrd,bgnd->bgrqn', qc, kcmp).astype(jnp.float32) * scale
        cvalid = cend[None, :] <= t[:, None]
        pc = jax.nn.softmax(jnp.where(cvalid, sc, NEG), axis=-1) * cvalid
        o_cmp = jnp.einsum('bgrqn,bgnd->bqgrd', pc.astype(vcmp.dtype), vcmp)
        imp = jnp.einsum('bgrqn,nj->bgqj', pc, overlap)
        tb = t // SEL_BLOCK
        forced = (jsel[None, :] == 0) | (jsel[None, :] == tb[:, None]) | (jsel[None, :] == tb[:, None] - 1)
        causal = sstart[None, :] <= t[:, None]
        imp = jnp.where(causal, jnp.where(forced, FORCE, imp), NEG)
        top_val, top_idx = lax.top_k(imp, n_sel)
        sel_ok = top_val > NEG * 0.5
        kg = ksb[bi, gi, top_idx]
        vg = vsb[bi, gi, top_idx]
        kpos = top_idx[..., None] * SEL_BLOCK + jnp.arange(SEL_BLOCK)
        dist = t[:, None, None] - kpos
        svalid = sel_ok[..., None] & (dist >= 0)
        bias = tab[gi[..., None], t5_bucket(dist)]
        ss = (jnp.einsum('bqgrd,bgqnkd->bgrqnk', qc, kg).astype(jnp.float32) * scale
              + jnp.moveaxis(bias, -1, 2).astype(jnp.float32))
        ss = jnp.where(svalid[:, :, None], ss, NEG)
        ps = jax.nn.softmax(ss.reshape(B, G, R, SEL_Q_CHUNK, n_sel * SEL_BLOCK), axis=-1)
        ps = ps.reshape(B, G, R, SEL_Q_CHUNK, n_sel, SEL_BLOCK)
        o_slc = jnp.einsum('bgrqnk,bgqnkd->bqgrd', ps.astype(vg.dtype), vg)
        return o_cmp, o_slc

    o_cmp, o_slc = lax.map(chunk, (qch, jnp.arange(nq)))
    o_cmp = jnp.moveaxis(o_cmp, 0, 1).reshape(B, S, G * R * Dh)
    o_slc = jnp.moveaxis(o_slc, 0, 1).reshape(B, S, G * R * Dh)
    return o_cmp, o_slc

def hybrid_mixer(xn, w_in, a_sinks, cmp_pos_k, cmp_w1_k, cmp_w2_k, cmp_pos_v, cmp_w1_v, cmp_w2_v,
                 w_br_a, w_br_b, w_out, rel_bias):
    B, S, _ = xn.shape
    proj = xn @ w_in
    offs = np.cumsum(IN_SIZES)[:-1].tolist()
    aq, ak, av, bq, bkc, bvc, bks, bvs, bkw, bvw, bg, mg = jnp.split(proj, offs, axis=-1)
    o_a = banded_attention(aq.reshape(B, S, A_KV, A_REP, HEAD_DIM),
                           ak.reshape(B, S, A_KV, HEAD_DIM), av.reshape(B, S, A_KV, HEAD_DIM),
                           A_WINDOW, A_BLOCK, rel_bias[:, :A_HEADS], a_sinks)
    qb = bq.reshape(B, S, B_KV, B_REP, HEAD_DIM)
    kv = lambda t: t.reshape(B, S, B_KV, HEAD_DIM)
    bias_b = rel_bias[:, A_HEADS:]
    o_cmp, o_slc = nsa_compressed_selected(qb, kv(bkc), kv(bvc), kv(bks), kv(bvs),
                                           cmp_pos_k, cmp_w1_k, cmp_w2_k, cmp_pos_v, cmp_w1_v, cmp_w2_v,
                                           bias_b)
    o_win = banded_attention(qb, kv(bkw), kv(bvw), B_WINDOW, B_WIN_BLOCK, bias_b, None)
    gates = jax.nn.sigmoid(bg.astype(jnp.float32)).reshape(B, S, B_HEADS, 3)
    heads = lambda o: o.reshape(B, S, B_HEADS, HEAD_DIM)
    o_b = (gates[..., 0:1] * heads(o_cmp) + gates[..., 1:2] * heads(o_slc)
           + gates[..., 2:3] * heads(o_win)).astype(xn.dtype).reshape(B, S, B_QW)
    g_a, g_b = jnp.split(jax.nn.sigmoid(mg), 2, axis=-1)
    merged = g_a * (o_a @ w_br_a) + g_b * (o_b @ w_br_b)
    return merged @ w_out

def hier_moe(xn, w_group, b_group, w_expert, b_expert, w1, w3, w2):
    B, S, D = xn.shape
    T = B * S
    xt = xn.reshape(T, D)
    glog = (xt @ w_group).astype(jnp.float32) + b_group.astype(jnp.float32)
    gprob = jax.nn.softmax(glog, axis=-1)
    gsel = jnp.argmax(glog, axis=-1).astype(jnp.int32)
    gw = jnp.take_along_axis(gprob, gsel[:, None], axis=-1)
    elog = ((xt @ w_expert).astype(jnp.float32) + b_expert.astype(jnp.float32)).reshape(T, N_GROUPS, EXPERTS_PER_GROUP)
    elog_g = jnp.take_along_axis(elog, gsel[:, None, None], axis=1)[:, 0]
    ev, ei = lax.top_k(elog_g, TOP_K_IN_GROUP)
    ew = jax.nn.softmax(ev, axis=-1) * gw
    eid = gsel[:, None] * EXPERTS_PER_GROUP + ei.astype(jnp.int32)
    A = T * TOP_K_IN_GROUP
    e_flat = eid.reshape(A)
    w_flat = ew.reshape(A)
    tok = jnp.repeat(jnp.arange(T, dtype=jnp.int32), TOP_K_IN_GROUP)
    order = jnp.argsort(e_flat)
    e_s, tok_s, w_s = e_flat[order], tok[order], w_flat[order]
    counts = jnp.zeros((N_EXPERTS,), jnp.int32).at[e_flat].add(1)
    starts = jnp.cumsum(counts) - counts
    padded = (counts + MOE_BLOCK - 1) // MOE_BLOCK * MOE_BLOCK
    pstarts = jnp.cumsum(padded) - padded
    dest = pstarts[e_s] + (jnp.arange(A, dtype=jnp.int32) - starts[e_s])
    P = A + N_EXPERTS * MOE_BLOCK
    nblk = P // MOE_BLOCK
    buf_tok = jnp.full((P,), T, jnp.int32).at[dest].set(tok_s)
    buf_w = jnp.zeros((P,), jnp.float32).at[dest].set(w_s)
    blk_expert = jnp.clip(jnp.searchsorted(pstarts + padded, jnp.arange(nblk) * MOE_BLOCK, side='right'),
                          0, N_EXPERTS - 1)
    x_pad = jnp.concatenate([xt, jnp.zeros((1, D), xt.dtype)], axis=0)
    xin = x_pad[buf_tok].reshape(nblk, MOE_BLOCK, D)

    def expert_block(args):
        xb, e = args
        return (jax.nn.silu(xb @ w1[e]) * (xb @ w3[e])) @ w2[e]

    y = lax.map(expert_block, (xin, blk_expert)).reshape(P, D)
    out = jax.ops.segment_sum(y.astype(jnp.float32) * buf_w[:, None], buf_tok, num_segments=T + 1)[:T]
    return out.astype(xn.dtype).reshape(B, S, D)

def setup_inputs(seed: int = 0) -> dict:
    key = jax.random.key(seed)
    keys = iter(jax.random.split(key, 24))
    nrm = lambda shape, scale: jax.random.normal(next(keys), shape, jnp.float32) * scale
    L = DEPTH
    return {
        "x": nrm((BATCH, SEQ, D_MODEL), 1.0),
        "rel_bias": nrm((N_BUCKETS, TOTAL_HEADS), 0.5),
        "norm_mix": 1.0 + nrm((L, D_MODEL), 0.1),
        "w_in": nrm((L, D_MODEL, IN_COLS), D_MODEL ** -0.5),
        "a_sinks": nrm((L, A_HEADS), 0.5),
        "cmp_pos_k": nrm((L, CMP_LEN, HEAD_DIM), 0.5),
        "cmp_w1_k": nrm((L, CMP_LEN * HEAD_DIM, CMP_HIDDEN), (CMP_LEN * HEAD_DIM) ** -0.5),
        "cmp_w2_k": nrm((L, CMP_HIDDEN, HEAD_DIM), CMP_HIDDEN ** -0.5),
        "cmp_pos_v": nrm((L, CMP_LEN, HEAD_DIM), 0.5),
        "cmp_w1_v": nrm((L, CMP_LEN * HEAD_DIM, CMP_HIDDEN), (CMP_LEN * HEAD_DIM) ** -0.5),
        "cmp_w2_v": nrm((L, CMP_HIDDEN, HEAD_DIM), CMP_HIDDEN ** -0.5),
        "w_br_a": nrm((L, A_QW, D_MODEL), A_QW ** -0.5),
        "w_br_b": nrm((L, B_QW, D_MODEL), B_QW ** -0.5),
        "w_out": nrm((L, D_MODEL, D_MODEL), D_MODEL ** -0.5),
        "norm_ffn": 1.0 + nrm((L, D_MODEL), 0.1),
        "w_group": nrm((L, D_MODEL, N_GROUPS), D_MODEL ** -0.5),
        "b_group": nrm((L, N_GROUPS), 0.01),
        "w_expert": nrm((L, D_MODEL, N_EXPERTS), D_MODEL ** -0.5),
        "b_expert": nrm((L, N_EXPERTS), 0.01),
        "w1": nrm((L, N_EXPERTS, D_MODEL, EXPERT_FF), D_MODEL ** -0.5),
        "w3": nrm((L, N_EXPERTS, D_MODEL, EXPERT_FF), D_MODEL ** -0.5),
        "w2": nrm((L, N_EXPERTS, EXPERT_FF, D_MODEL), EXPERT_FF ** -0.5),
        "norm_final": 1.0 + nrm((D_MODEL,), 0.1),
    }

def reference(x, rel_bias, norm_mix, w_in, a_sinks, cmp_pos_k, cmp_w1_k, cmp_w2_k, cmp_pos_v, cmp_w1_v, cmp_w2_v,
              w_br_a, w_br_b, w_out, norm_ffn, w_group, b_group, w_expert, b_expert, w1, w3, w2, norm_final):
    h = x
    for l in range(DEPTH):
        hn = rmsnorm(h, norm_mix[l])
        h = h + hybrid_mixer(hn, w_in[l], a_sinks[l], cmp_pos_k[l], cmp_w1_k[l], cmp_w2_k[l],
                             cmp_pos_v[l], cmp_w1_v[l], cmp_w2_v[l], w_br_a[l], w_br_b[l], w_out[l], rel_bias)
        hn = rmsnorm(h, norm_ffn[l])
        h = h + hier_moe(hn, w_group[l], b_group[l], w_expert[l], b_expert[l], w1[l], w3[l], w2[l])
    return rmsnorm(h, norm_final)


_drawn_inputs = setup_inputs


def setup_inputs(seed=0):
    import zlib

    import numpy as np

    out = dict(_drawn_inputs(seed))
    spreads = {}
    factors = {'a_sinks': 6.97, 'b_group': 3.968, 'b_expert': 4.384}
    for name, (base, spread) in spreads.items():
        noise = np.random.default_rng([zlib.crc32(name.encode()), seed]).standard_normal(out[name].shape)
        drawn = base * np.exp(spread * noise) if base else spread * noise
        out[name] = __import__('jax').numpy.asarray(drawn.astype(out[name].dtype))
    for name, factor in factors.items():
        out[name] = (out[name] * factor).astype(out[name].dtype)
    return out
```

```python
from contextlib import ExitStack

import numpy as np

import concourse.bass as bass
from concourse import mybir

F32 = mybir.dt.float32
BF16 = mybir.dt.bfloat16
I32 = mybir.dt.int32
ALU = mybir.AluOpType
ACT = mybir.ActivationFunctionType
X = mybir.AxisListType.X

P = 128
SEQ = 1024
D = 1024
DH = 64
REP = 4
WIN_BLOCKS = 4
NB = 63
NE = 32
NG = 4
EPG = NE // NG
FF = 512
TT = SEQ // P
KT = D // P
SLOTS = 64
MAXB = NE + 2 * SEQ // SLOTS
EPS = 1e-5
NEG = -1e30
SC = DH ** -0.5
GELU_C = 0.7978845608028654

AQ, AK, AV, BQ, BKC, BVC, BKS, BVS, BKW, BVW, BG, MG = 0, 512, 640, 768, 1280, 1408, 1536, 1664, 1792, 1920, 2048, 2072
VG_W = 3 * P + 24
RV = 384


def shape_constants():
    dist = 255 - np.arange(RV)
    n = np.maximum(dist, 0)
    large = 16 + (np.log(np.maximum(n, 1).astype(np.float32) / np.float32(16)) / np.float32(np.log(128 / 16))
                  * np.float32(16)).astype(np.int32)
    bucket = np.where(n < 16, n, np.minimum(large, 31))
    hot = np.zeros((32, RV), np.float32)
    hot[bucket, np.arange(RV)] = 8.0
    hot_b = hot.copy()
    hot_b[31, :] -= 8.0
    mask = np.zeros((8, 2, RV), np.float32)
    mask[:, 0, (dist < 0) | (dist >= 128)] = 8 * NEG
    mask[:, 1, dist < 0] = 8 * NEG
    return np.stack([hot, hot_b], 1), mask


def attention_units():
    units = []
    for i in range(TT):
        units += [(i, "A", r, list(range(max(0, i - 1), i + 1))) for r in range(REP)]
        units += [(i, "C", 0, [0])]
        units += [(i, "W", h, list(range(max(0, i - WIN_BLOCKS), i + 1))) for h in range(2 * REP)]
        units += [(i, "S", h, list(range(i + 1))) for h in range(2 * REP)]
    return units


def build(nc, t, out):
    ctx = ExitStack()

    def sb(name, shape, dt=F32):
        return ctx.enter_context(nc.sbuf_tensor(name, shape, dt))

    def sem(name):
        return ctx.enter_context(nc.semaphore(name))

    def scratch(name, shape):
        return nc.dram_tensor(name, shape, F32, kind="Internal").ap()

    rvec_d = scratch("rvec_d", (16, P, RV))
    h2_d = scratch("h2_d", (SEQ, D))
    rows_d = scratch("rows_d", ((MAXB + 1) * SLOTS, D))

    WA = sb("WA", [P, 24576])
    BA = sb("BA", [P, 25600])

    def wa(a, b, pat=None, /, **kw):
        v = WA[:, a:b]
        return v.rearrange(pat, **kw) if pat else v

    def ba(a, b, pat=None, /, **kw):
        v = BA[:, a:b]
        return v.rearrange(pat, **kw) if pat else v

    hnT = wa(0, 8192, "p (k t) -> p k t", k=KT)
    qa = wa(8192, 12288, "p (r t) -> p r t", r=REP)
    qb = wa(12288, 16384, "p (r t) -> p r t", r=REP)
    kz = wa(16384, 22528, "p (w g t) -> p w g t", w=3, g=2)
    xt = wa(22528, 24576, "p (b n) -> p b n", b=2)
    bias = ba(0, 4096, "p (h k) -> p h k", h=16)
    vgw = ba(0, KT * VG_W, "p (k n) -> p k n", k=KT)
    gel = ba(3264, 3264 + 3 * 252, "p (x n) -> p x n", x=3)
    v_sb = ba(4096, 7168, "p (w t n) -> p w t n", w=3, t=TT)
    c2 = ba(7168, 11264, "p (w g t) -> p w g t", w=2, g=2)
    xblk = ba(11264, 11264 + 2016, "p (l g n) -> p l g n", l=16, g=2)
    w1c = ba(13312, 17408, "p (l h) -> p l h", l=16)
    xs = ba(17408, 19456, "p (b n) -> p b n", b=2)
    ws = ba(19456, 25600, "p (s k n) -> p s k n", s=6, k=KT)
    pT = ba(7168, 22528, "p (s g r t) -> p s g r t", s=15, g=2, r=REP)
    PB = ba(22528, 25600, "p (b n) -> p b n", b=3)
    SLOT0 = {"S": 0, "W": 8, "A": 13}

    wout = ba(0, 8192, "p (k n) -> p k n", k=KT)
    mT = ba(8192, 16384, "p (t k n) -> p t k n", t=TT, k=KT)
    h2T = ba(16384, 18432, "p (b k n) -> p b k n", b=2, k=KT)
    gff = ba(18432, 19456)
    tmp = wa(16384, 20480, "p (b x n) -> p b x n", b=2, x=4)
    xr = ba(19456, 21504, "p (b n) -> p b n", b=2)
    h2 = ba(21504, 23552, "p (b n) -> p b n", b=2)
    junk = ba(23552, 24576)

    ident = sb("ident", [P, P])
    tri = sb("tri", [P, P], BF16)
    ones = sb("ones", [P, P], BF16)
    winmask = sb("winmask", [P, P], BF16)
    cmpmask = sb("cmpmask", [P, TT, 64], BF16)
    gT = sb("gT", [P, KT])
    pos = sb("pos", [P, 2, 16])
    w2c = sb("w2c", [P, 2, 2, DH])
    kcz = sb("kcz", [P, P])
    vcz = sb("vcz", [P, P])
    pc = sb("pc", [P, 8, 64])
    pcT = sb("pcT", [P, REP, P])
    gates = sb("gates", [P, TT, 24])
    tab = sb("tab", [32, 16])
    sinks = sb("sinks", [P, 2, REP])
    nsink = sb("nsink", [P, 2, REP])
    eps_t = sb("eps_t", [P, 1])
    stat = sb("stat", [P, 3, TT])
    rowok = sb("rowok", [P, 1])
    mx = sb("mx", [P, 4, 8])
    ngm = sb("ngm", [P, 4, 2])
    den = sb("den", [P, 4, 8])
    esk = sb("esk", [P, 4, 2])
    rin = sb("rin", [P, 4, 8])
    slots_i = sb("slots_i", [P, 2, TT], I32)
    tokw = sb("tokw", [P, 2, TT])
    starts_i = sb("starts_i", [P, NE + 1], I32)
    PS = ctx.enter_context(nc.psum_tensor("PS", [P, 8, 512], F32))

    names = """small_in x_in0 x_in1 const_ready std_done xs_ready xT_ps hnT_done
        w_in0 w_in1 w_in2 w_in3 w_in4 w_in5 vg_in w1_in0 w1_in1 proj_ps proj_act proj_dve 
        kz_zero bias_ps bias_vec bias_out bias_in dve_step pool_step xblk_done hid_ps gelu_act gelu_dve cmp_ps cmp_done
        s_ready front exp_done back scaled t_done evac_act evac_dve pv_done o_evac
        m_in0 m_in1 merge_ps gate_act merge_dve wout_in gff_in xr_in0 xr_in1 out_ps h2_done h2_std
        hn2_done h2T_ps h2T_done log_ps log_done zero_done routed scattered wr_in
        we0 we1 we2 we3 we4 we5 x_blk x_tr xT_evac mm1 mm3 tanh_done hid_done hT_ps hT_done y_ps y_evac y_st
        g_in0 g_in1 comb_std comb_done out_st0 out_st1 act_step h2_st0 h2_st1 gate_in hu_done loop_left gelu_arg tanh_gates nsink_done comb_sum gfin_in assigned route_arg route_exp route_ps masks_ready tables y_free""".split()
    S = {n: sem(n) for n in names}
    block = ctx.enter_context(nc.Block())

    w_in = t["w_in"]
    w_in_k = w_in.rearrange("(k p) n -> p k n", p=P)
    blocks = [("kc", BKC, BKC + 64), ("vc", BVC, BVC + 64)]
    blocks += [(f"qb{r}", BQ + 64 * r, BQ + 256 + 64 * r) for r in range(REP)]
    blocks += [("ks", BKS, BKS + 64), ("kw", BKW, BKW + 64)]
    blocks += [(f"qa{r}", AQ + 64 * r, AQ + 256 + 64 * r) for r in range(REP)]
    blocks += [("ka", AK, AK + 64)]
    NBLK = len(blocks)
    jobs = [(name, c, hf) for c, (name, _, _) in enumerate(blocks) for hf in range(2)]
    jobs = jobs[:4] + [("vg", 0, i) for i in range(TT)] + jobs[4:]
    job_of = {c: j for j, (name, c, h) in enumerate(jobs) if name != "vg" and h == 1}
    units = attention_units()
    NU = len(units)
    groups, first_group = [], []
    for u, (i, br, h, kbs) in enumerate(units):
        first_group.append(len(groups))
        if br == "A":
            groups.append((u, [(g, kb) for kb in range(len(kbs)) for g in range(2)]))
        elif br == "C":
            groups.append((u, [(0, r) for r in range(REP)]))
        else:
            for a in range(0, len(kbs), 4):
                groups.append((u, [(h // REP, kb) for kb in range(a, min(a + 4, len(kbs)))]))
    first_group.append(len(groups))
    last_of = {}
    for u, (i, br, h, kbs) in enumerate(units):
        last_of[(i, br)] = u
    pv_order = [(i, br) for i in range(TT) for br in "ACWS"]

    def groups_before(n, parity):
        return (n + 1 - parity) // 2

    xin = ba(8192, 8704)
    xT = ba(9216, 9728, "p (k n) -> p k n", k=KT)
    xT_out = xT.rearrange("p (h c) n -> p c h n", h=2)
    xT_ps = PS[:, 7, :].rearrange("p (c h n) -> p c h n", c=4, h=2)
    th = ba(9728, 9984)
    hu = ba(9984, 10240)
    hv = ba(10240, 10496)
    hT = ba(10496, 10752, "p (j n) -> p j n", j=2)
    ysb = ba(10752, 11264)
    fin_h = ba(12288, 14336, "p (b n) -> p b n", b=2)
    fin_y = ba(14336, 18432, "p (b k n) -> p b k n", b=2, k=2)
    gfin = ba(18432, 19456)
    fin_o = ba(19456, 21504, "p (b n) -> p b n", b=2)
    fjunk = ba(21504, 22528)
    W1 = [wa(12288 * b, 12288 * b + 4096, "p (k n) -> p k n", k=KT) for b in range(2)]
    W3 = [wa(12288 * b + 4096, 12288 * b + 8192, "p (k n) -> p k n", k=KT) for b in range(2)]
    W2 = [wa(12288 * b + 8192, 12288 * b + 12288, "p (k n) -> p k n", k=4) for b in range(2)]
    hot = WA[0:32, 8192:8960].rearrange("p (w n) -> p w n", w=2)
    hmask = WA[0:8, 8960:9728].rearrange("p (w n) -> p w n", w=2)
    tab_vec = WA[0:8, 9728:10496].rearrange("p (w n) -> p w n", w=2)
    lg = ba(0, 288, "p (t n) -> p t n", t=TT)
    G4 = [ba(288 + 32 * j, 320 + 32 * j, "p (t n) -> p t n", t=TT) for j in range(6)]
    G8 = [ba(480 + 8 * j, 488 + 8 * j) for j in range(20)]
    G32 = [ba(640 + 256 * j, 896 + 256 * j, "p (t n) -> p t n", t=TT) for j in range(8)]
    onehot = [ba(2688 + 256 * j, 2944 + 256 * j, "p (t n) -> p t n", t=TT) for j in range(2)]
    rev32 = ba(3200, 3232)
    rev4 = ba(3232, 3236)
    lim = ba(3236, 3251)
    upto = ba(3264, 4288, "p (e f) -> p e f", e=NE)
    big = ba(4288, 5312, "p (e f) -> p e f", e=NE)
    cnt = ba(5312, 5344)
    nblk = ba(5344, 5376)
    starts_f = ba(5376, 5376 + NE + 1)
    base32 = ba(5440, 5472)
    offs = ba(5472, 5728, "p (t n) -> p t n", t=TT)
    assign = sb("assign", [P, 2 * P], BF16)
    wr = ba(23552, 24320, "p (k n) -> p k n", k=KT)
    rbias = ba(24320, 24356)
    junk2 = ba(24576, 25600)

    def load_expert(sp, e, par):
        for j, (name, dst, k) in enumerate((("w1", W1, KT), ("w3", W3, KT), ("w2", W2, 4))):
            src = t[name].rearrange("e (k p) n -> e p k n", p=P)[bass.ds(e, 1)].rearrange("e p k n -> (e p) k n")
            sp.dma_start(dst[par][:, :, :], src).then_inc(S[f"we{3 * par + j}"], 16)

    def store_out(sp, i):
        sp.wait_ge(S["comb_done"], i + 1)
        sp.dma_start(out.rearrange("b t n -> (b t) n")[P * i:P * i + P, :], fin_o[:, i % 2, :]).then_inc(S[f"out_st{i % 2}"], 16)

    SMALL = [(gT[:, :], t["norm_mix"].rearrange("(k p) -> p k", p=P)),
             (tab[:, :], t["rel_bias"]),
             (hot[:, :, :], t["bucket_hot"]),
             (hmask[:, :, :], t["distance_mask"]),
             (sinks[:, :, :].rearrange("p g r -> p (g r)"), t["a_sinks"].partition_broadcast(P))]
    for w, c in enumerate("kv"):
        SMALL += [(pos[:, w, :], t[f"cmp_pos_{c}"].rearrange("(l two) d -> (two d) l", two=2)),
                  (w2c[:, w, :, :], t[f"cmp_w2_{c}"].rearrange("(h p) d -> p h d", p=P))]
    NSMALL = len(SMALL)
    lgs = sb("lgs", [P, TT, NG + NE])

    def evacuate(eng, name, c, h, bank, copy):
        ps = PS[:, bank, :]
        tk = 512 * h
        if name in ("kc", "vc"):
            w = "kv".index(name[0])
            cut = 1 if h == 0 else 0
            for g in range(2):
                src = ps[DH * g:DH * g + DH, :]
                yield copy(c2[0:DH, w, g, tk:tk + 512], src)
                yield copy(c2[DH:P, w, g, tk - 1 + cut:tk + 511], src[:, cut:512])
        elif name in ("ka", "ks", "kw"):
            for g in range(2):
                yield copy(kz[DH * g:DH * g + DH, "asw".index(name[1]), g, tk:tk + 512], ps[DH * g:DH * g + DH, :])
        elif name == "vg":
            yield copy(v_sb[:, :, h, :], ps[:, 0:3 * P].rearrange("p (w n) -> p w n", w=3))
            yield copy(gates[:, h, :], ps[:, 3 * P:VG_W])
        else:
            if name == "qa0":
                eng.wait_ge(S["bias_out"], 32)
            yield copy((qa if name[1] == "a" else qb)[:, int(name[2]), tk:tk + 512], ps)

    def group_copies(n):
        u, members = groups[n]
        i, br, h, kbs = units[u]
        ps = PS[:, 4 + n % 2, :].rearrange("p (m t) -> p m t", t=P)
        if br == "C":
            return [(pcT[:, :, :], ps)]
        if br == "A":
            return [(pT[:, SLOT0["A"] + kb, :, h, :], ps[:, 2 * kb:2 * kb + 2, :]) for kb in range(len(kbs))]
        g, r, kb0 = h // REP, h % REP, members[0][1]
        s = SLOT0[br] + kb0
        return [(pT[:, s:s + len(members), g, r, :], ps[:, 0:len(members), :])]

    def slot_free(eng, n):
        i, br = units[groups[n][0]][:2]
        if i >= 1:
            eng.wait_ge(S["pv_done"], pv_order.index((i - 1, br)) + 1)

    @block.sync
    def _(sp):
        x_k = t["x"].rearrange("b (t p) n -> (b t) p n", p=P)
        for i in range(TT):
            if i >= 2:
                sp.wait_ge(S["xs_ready"], i - 1)
            sp.dma_start(xt[:, i % 2, :], x_k[i]).then_inc(S[f"x_in{i % 2}"], 16)
            if i == 1:
                for c in range(6):
                    for j in range(2):
                        sp.dma_start(ws[:, c, :, 64 * j:64 * j + 64],
                                     w_in_k[:, :, blocks[c][1 + j]:blocks[c][1 + j] + 64]).then_inc(S[f"w_in{c}"], 16)
                for j, a in enumerate((AV, BVS, BVW)):
                    sp.dma_start(vgw[:, :, P * j:P * j + P], w_in_k[:, :, a:a + P]).then_inc(S["vg_in"], 16)
                sp.dma_start(vgw[:, :, 3 * P:VG_W], w_in_k[:, :, BG:BG + 24]).then_inc(S["vg_in"], 16)
        sp.dma_start(w1c[:, :, :], t["cmp_w1_k"].rearrange("(l p) h -> p l h", p=P)).then_inc(S["w1_in0"], 16)
        for c in range(6, NBLK):
            sp.wait_ge(S["proj_ps"], job_of[c - 6] + 1)
            for j in range(2):
                sp.dma_start(ws[:, c % 6, :, 64 * j:64 * j + 64],
                             w_in_k[:, :, blocks[c][1 + j]:blocks[c][1 + j] + 64]).then_inc(S[f"w_in{c % 6}"], 16)
            if c == 9:
                sp.wait_ge(S["hid_ps"], 1)
                sp.dma_start(w1c[:, :, :], t["cmp_w1_v"].rearrange("(l p) h -> p l h", p=P)).then_inc(S["w1_in1"], 16)
        sp.wait_ge(S["bias_vec"], 2)
        for w in range(2):
            sp.dma_start(rvec_d[8 * w:8 * w + 8], tab_vec[:, w, :].unsqueeze(1).to_broadcast([8, P, RV])) \
                .then_inc(S["bias_out"], 16)
        sp.wait_ge(S["bias_out"], 32)
        sp.wait_ge(S["cmp_ps"], 2)
        toeplitz = bass.AP(rvec_d.tensor, rvec_d.offset + P - 1, [[RV - 1, P], [P * RV, 16], [1, 256]])
        sp.dma_start(bias[:, :, :], toeplitz).then_inc(S["bias_in"], 16)

        sp.wait_ge(S["kz_zero"], 2)
        with sp.Fori(0, MAXB + 1) as b:
            sp.dma_start(rows_d[bass.ds(b * SLOTS, SLOTS), :], kz[DH:P, 0, 0, :]).then_inc(S["zero_done"], 16)

        wbr = [t[n].rearrange("(g r d) n -> g d r n", g=2, r=REP) for n in ("w_br_a", "w_br_b")]
        sp.wait_ge(S["t_done"], len(groups))
        sp.wait_ge(S["pv_done"], len(pv_order))
        for dt in range(KT):
            b = dt % 2
            if dt >= 2:
                sp.wait_ge(S["merge_ps"], 2 * (dt - 1))
            for j in range(2):
                sp.dma_start(ws[:, 3 * b + j, :, :],
                             w_in_k[:, :, MG + D * j + P * dt:MG + D * j + P * dt + P]).then_inc(S[f"m_in{b}"], 16)
            for j in range(2):
                for g in range(2):
                    sp.dma_start(ws[DH * g:DH * g + DH, 3 * b + 2, 4 * j:4 * j + 4, :],
                                 wbr[j][g, :, :, P * dt:P * dt + P]).then_inc(S[f"m_in{b}"], 16)
            if dt == 2:
                sp.dma_start(wout[:, :, :], t["w_out"].rearrange("(k p) n -> p k n", p=P)).then_inc(S["wout_in"], 16)
                sp.dma_start(gff, t["norm_ffn"].partition_broadcast(P)).then_inc(S["gff_in"], 16)
        sp.wait_ge(S["merge_ps"], 2 * KT)
        for i in range(TT):
            if i >= 2:
                sp.wait_ge(S["h2_done"], i - 1)
            sp.dma_start(xr[:, i % 2, :], x_k[i]).then_inc(S[f"xr_in{i % 2}"], 16)
            if i == 1:
                sp.wait_ge(S["merge_dve"], 2 * KT)
                for e in range(2):
                    load_expert(sp, e, e)
            if i >= 1:
                sp.wait_ge(S["h2_done"], i)
                sp.dma_start(h2_d[P * (i - 1):P * i, :], h2[:, (i - 1) % 2, :]).then_inc(S[f"h2_st{(i - 1) % 2}"], 16)
        sp.wait_ge(S["h2_done"], TT)
        sp.dma_start(h2_d[SEQ - P:SEQ, :], h2[:, (TT - 1) % 2, :]).then_inc(S[f"h2_st{(TT - 1) % 2}"], 16)
        sp.wait_ge(S["routed"], 1)
        with sp.Fori(1, NE // 2) as e2:
            for par in range(2):
                used = sp.value_load(starts_i[0:1, bass.ds(e2 * 2 + par - 1, 1)], min_val=1, max_val=MAXB)
                sp.wait_ge(S["y_ps"], used)
                load_expert(sp, e2 * 2 + par, par)
        for b in range(2):
            sp.wait_ge(S[f"h2_st{b}"], 16 * TT // 2)
        sp.wait_ge(S["loop_left"], 1)
        for i in range(TT):
            if i >= 2:
                sp.wait_ge(S["comb_done"], i - 1)
            sp.dma_start(fin_h[:, i % 2, :], h2_d[P * i:P * i + P, :]).then_inc(S[f"xr_in{i % 2}"], 16)
            if i >= 1:
                store_out(sp, i - 1)
        store_out(sp, TT - 1)
        for b in range(2):
            sp.wait_ge(S[f"out_st{b}"], 16 * TT // 2)


    @block.tensor
    def _(pe):
        def evacuated(j):
            if j >= 4:
                pe.wait_ge(S["proj_act" if j % 2 == 0 else "proj_dve"], (j - 4) // 2 + 1)

        pe.wait_ge(S["const_ready"], 1)
        for i in range(TT):
            pe.wait_ge(S["xs_ready"], i + 1)
            if i >= 2:
                pe.wait_ge(S["hnT_done"], i - 1)
            for k in range(KT):
                mm = pe.transpose(PS[:, 2 * (i % 2) + k // 4, P * (k % 4):P * (k % 4) + P],
                                  xs[:, i % 2, P * k:P * k + P], ident[:, :])
            mm.then_inc(S["xT_ps"], 1)
        pe.wait_ge(S["small_in"], 16 * NSMALL)
        for w in range(2):
            mm = pe.matmul(PS[0:8, 4 + w, 0:RV], tab[:, 8 * w:8 * w + 8], hot[:, w, :], start=True, stop=True)
        mm.then_inc(S["bias_ps"], 1)
        pe.wait_ge(S["hnT_done"], TT)

        def hidden(w):
            pe.wait_ge(S["xblk_done"], w + 1)
            pe.wait_ge(S[f"w1_in{w}"], 16)
            for ht in range(2):
                for l in range(16):
                    mm = pe.matmul(PS[:, 6 + w, 126 * ht:126 * ht + 126], w1c[:, l, P * ht:P * ht + P],
                                   xblk[:, l, :, :], start=(l == 0), stop=(l == 15))
            mm.then_inc(S["hid_ps"], 1)

        for j, (name, c, h) in enumerate(jobs):
            evacuated(j)
            if name == "vg":
                if h == 0:
                    pe.wait_ge(S["vg_in"], 64)
                for k in range(KT):
                    mm = pe.matmul(PS[:, j % 4, 0:VG_W], hnT[:, k, P * h:P * h + P], vgw[:, k, :],
                                   start=(k == 0), stop=(k == KT - 1))
            else:
                pe.wait_ge(S[f"w_in{c % 6}"], 32 * (c // 6 + 1))
                for k in range(KT):
                    mm = pe.matmul(PS[:, j % 4, :], ws[:, c % 6, k, :], hnT[:, k, 512 * h:512 * h + 512],
                                   start=(k == 0), stop=(k == KT - 1))
            mm.then_inc(S["proj_ps"], 1)
            if j == 11:
                hidden(0)
            if j == 19:
                pe.wait_ge(S["gelu_dve"], 1)
                for ht in range(2):
                    mm = pe.matmul(PS[0:DH, 4, 0:126], w2c[:, 0, ht, :], gel[:, 2, 126 * ht:126 * ht + 126],
                                   start=(ht == 0), stop=(ht == 1))
                mm.then_inc(S["cmp_ps"], 1)
            if j == 27:
                hidden(1)
        pe.wait_ge(S["gelu_dve"], 2)
        for g in range(2):
            for ht in range(2):
                mm = pe.matmul(PS[0:NB, 5, DH * g:DH * g + DH], gel[:, 2, 126 * ht + NB * g:126 * ht + NB * g + NB],
                               w2c[:, 1, ht, :], start=(ht == 0), stop=(ht == 1))
        mm.then_inc(S["cmp_ps"], 1)

        def scores(u):
            i, br, h, kbs = units[u]
            b0, n = 2 * (u % 2), P * len(kbs)
            k0 = P * kbs[0]
            if u >= 2:
                pe.wait_ge(S["exp_done"], u - 1)
            if u == 0:
                pe.wait_ge(S["proj_act"], len(jobs) // 2)
                pe.wait_ge(S["proj_dve"], len(jobs) // 2)
                pe.wait_ge(S["cmp_done"], 2)
            q = slice(P * i, P * i + P)
            if br == "A":
                mm = pe.matmul(PS[:, b0, 0:2 * n], qa[:, h, q], kz[:, 0, :, k0:k0 + n], start=True, stop=True)
            elif br == "C":
                for r in range(REP):
                    mm = pe.matmul(PS[:, b0, P * r:P * r + P], qb[:, r, q], kcz[:, :], start=True, stop=True)
            else:
                g, r = h // REP, h % REP
                w = 1 if br == "S" else 2
                for a in range(0, n, 512):
                    e = min(n, a + 512)
                    mm = pe.matmul(PS[:, b0 + a // 512, 0:e - a], qb[:, r, q], kz[:, w, g, k0 + a:k0 + e],
                                   start=True, stop=True)
            mm.then_inc(S["s_ready"], 1)

        def turn(u):
            i, br, h, kbs = units[u]
            pe.wait_ge(S["scaled"], u + 1)
            for n in range(first_group[u], first_group[u + 1]):
                if n >= 2:
                    pe.wait_ge(S["evac_act" if n % 2 == 0 else "evac_dve"], n // 2)
                for m, (g, kb) in enumerate(groups[n][1]):
                    if br == "A":
                        src = PB[:, u % 3, P * (len(kbs) * g + kb):P * (len(kbs) * g + kb) + P]
                    elif br == "C":
                        src = pc[:, 2 * kb:2 * kb + 2, :]
                    else:
                        src = PB[:, u % 3, P * kb:P * kb + P]
                    mm = pe.transpose(PS[:, 4 + n % 2, P * m:P * m + P], src, ident[:, :])
                mm.then_inc(S["t_done"], 1)

        def values(i, br):
            m = last_of[(i, br)]
            done = first_group[m + 1]
            pe.wait_ge(S["evac_act"], groups_before(done, 0))
            pe.wait_ge(S["evac_dve"], groups_before(done, 1))
            kbs = units[m][3]
            if br in "AC" and i >= 1:
                pe.wait_ge(S["o_evac"], 2 * i - (1 if br == "A" else 0))
            if br == "C":
                mm = pe.matmul(PS[:, 7, :], vcz[:, :], pcT[:, :, :], start=True, stop=True)
            else:
                bank, w = (6, 0) if br == "A" else (7, 1 if br == "S" else 2)
                for n, kb in enumerate(kbs):
                    for g in range(2):
                        mm = pe.matmul(PS[DH * g:DH * g + DH, bank, :], v_sb[:, w, kb, DH * g:DH * g + DH],
                                       pT[:, SLOT0[br] + n, g, :, :], start=(br == "A" and n == 0),
                                       stop=(br != "A" or n == len(kbs) - 1), skip_group_check=True)
            mm.then_inc(S["pv_done"], 1)

        for n in range(NU + 3):
            if n < NU:
                scores(n)
            if 2 <= n < NU + 2:
                turn(n - 2)
            if n >= 3 and (n - 3) == last_of[units[n - 3][:2]]:
                values(*units[n - 3][:2])

        for dt in range(KT):
            for hf in range(2):
                pi = 2 * dt + hf
                b0 = 4 * (pi % 2)
                if pi == 0:
                    pe.wait_ge(S["o_evac"], 2 * TT)
                if pi >= 2:
                    pe.wait_ge(S["merge_dve"], pi - 1)
                if hf == 0:
                    pe.wait_ge(S[f"m_in{dt % 2}"], 96 * (dt // 2 + 1))
                sl = slice(512 * hf, 512 * hf + 512)
                for j in range(2):
                    for k in range(KT):
                        mm = pe.matmul(PS[:, b0 + j, :], ws[:, 3 * (dt % 2) + j, k, :], hnT[:, k, sl],
                                       start=(k == 0), stop=(k == KT - 1))
                mm.then_inc(S["gate_in"], 1)
                for j, o in enumerate((qa, qb)):
                    for r in range(REP):
                        mm = pe.matmul(PS[:, b0 + 2 + j, :], ws[:, 3 * (dt % 2) + 2, 4 * j + r, :], o[:, r, sl],
                                       start=(r == 0), stop=(r == REP - 1))
                mm.then_inc(S["merge_ps"], 1)

        def router(i):
            pe.wait_ge(S["hn2_done"], i + 1)
            if i >= 1:
                pe.wait_ge(S["h2T_done"], i)
            for k in range(KT):
                mm = pe.transpose(PS[:, 4 + k // 4, P * (k % 4):P * (k % 4) + P], mT[:, i, k, :], ident[:, :])
            mm.then_inc(S["h2T_ps"], 1)
            pe.wait_ge(S["h2T_done"], i + 1)
            if i == 0:
                pe.wait_ge(S["wr_in"], 64)
            if i >= 1:
                pe.wait_ge(S["log_done"], i)
            for k in range(KT):
                mm = pe.matmul(PS[:, 6, 0:96], h2T[:, i % 2, k, :], wr[:, k, :], start=(k == 0), stop=(k == KT - 1))
            mm.then_inc(S["log_ps"], 1)

        pe.wait_ge(S["wout_in"], 16)
        pe.wait_ge(S["merge_dve"], 2 * KT)
        for i in range(TT + 1):
            if i < TT:
                if i >= 2:
                    pe.wait_ge(S["h2_done"], i - 1)
                for n in range(2):
                    for k in range(KT):
                        mm = pe.matmul(PS[:, 2 * (i % 2) + n, :], mT[:, i, k, :], wout[:, k, 512 * n:512 * n + 512],
                                       start=(k == 0), stop=(k == KT - 1))
                mm.then_inc(S["out_ps"], 1)
            if i >= 1:
                router(i - 1)

        pe.wait_ge(S["assigned"], 1)
        pe.matmul(PS[:, 0, 0:256], tri[:, :], assign[:, :], start=True, stop=True)
        pe.matmul(PS[:, 1, 0:256], ones[:, :], assign[:, :], start=True, stop=True).then_inc(S["route_ps"], 1)

        def turn_rows():
            for c in range(4):
                mm = pe.transpose(PS[:, 7, P * c:P * c + P], xin[:, P * c:P * c + P], ident[:, :])
            mm.then_inc(S["x_tr"], 1)

        pe.wait_ge(S["routed"], 1)
        pe.wait_ge(S["x_blk"], 32)
        turn_rows()

        def expert(e, nth, par):
            lo = pe.value_load(starts_i[0:1, bass.ds(e, 1)], min_val=0, max_val=MAXB)
            hi = pe.value_load(starts_i[0:1, bass.ds(e + 1, 1)], min_val=1, max_val=MAXB)
            landed = pe.snap(nth * 16)
            with pe.Fori(lo, hi) as b:
                rows_in = pe.snap(b * 32 + 64)
                pe.wait_ge(S["xT_evac"], b + 1)
                for bank, w in ((0, W1), (1, W3)):
                    pe.wait_ge(S[f"we{3 * par + bank}"], landed)
                    for k in range(KT):
                        for h in range(2):
                            mm = pe.matmul(PS[DH * h:DH * h + DH, bank, 0:256], xT[:, k, :],
                                           w[par][:, k, 256 * h:256 * h + 256], start=(k == 0), stop=(k == KT - 1))
                    mm.then_inc(S["mm1" if bank == 0 else "mm3"], 1)
                pe.wait_ge(S["hid_done"], b + 1)
                for j in range(2):
                    mm = pe.transpose(PS[:, 2, P * j:P * j + P], hv[:, P * j:P * j + P], ident[:, :])
                mm.then_inc(S["hT_ps"], 1)
                pe.wait_ge(S["x_blk"], rows_in)
                turn_rows()
                pe.wait_ge(S["hT_done"], b + 1)
                pe.wait_ge(S[f"we{3 * par + 2}"], landed)
                for f in range(4):
                    for n in range(2):
                        mm = pe.matmul(PS[DH * n:DH * n + DH, 3, :], hT[:, f % 2, SLOTS * (f // 2):SLOTS * (f // 2) + SLOTS],
                                       W2[par][:, f, 512 * n:512 * n + 512], start=(f == 0), stop=(f == 3))
                mm.then_inc(S["y_ps"], 1)

        with pe.Fori(0, NE // 2) as e2:
            for par in range(2):
                expert(e2 * 2 + par, e2 + 1, par)

    @block.scalar
    def _(act):
        for dst, src in SMALL:
            act.dma_start(dst, src, allow_slow_non_contiguous=True).then_inc(S["small_in"], 16)
        act.wait_ge(S["const_ready"], 1)
        for i in range(TT):
            act.wait_ge(S[f"x_in{i % 2}"], 16 * (i // 2 + 1))
            nc.scalar.activation(PS[:, 6:8, :], xt[:, i % 2, :].rearrange("p (a n) -> p a n", a=2), ACT.Square,
                                 accum_out=stat[:, 0, i:i + 1]).then_inc(S["act_step"], 1)
            act.wait_ge(S["act_step"], i + 1)
            nc.scalar.activation(stat[:, 1, i:i + 1], stat[:, 0, i:i + 1], ACT.Sqrt, bias=eps_t[:, :],
                                 scale=1.0 / D).then_inc(S["std_done"], 1)

        for j, (name, c, h) in enumerate(jobs):
            if j % 2 == 0:
                act.wait_ge(S["proj_ps"], j + 1)
                for ins in evacuate(act, name, c, h, j % 4, nc.scalar.copy):
                    last = ins
                last.then_inc(S["proj_act"], 1)
            if j in (15, 29):
                w = 0 if j == 15 else 1
                act.wait_ge(S["gelu_arg"], w + 1)
                nc.scalar.activation(gel[:, 1, :], gel[:, 0, :], ACT.Tanh, scale=GELU_C).then_inc(S["gelu_act"], 1)
        act.wait_ge(S["proj_dve"], len(jobs) // 2)
        act.wait_ge(S["proj_act"], len(jobs) // 2)
        nc.scalar.activation(gates[:, :, :], gates[:, :, :], ACT.Tanh, scale=0.5).then_inc(S["tanh_gates"], 1)

        def move_group(n):
            act.wait_ge(S["t_done"], n + 1)
            slot_free(act, n)
            for dst, src in group_copies(n):
                last = nc.scalar.copy(dst, src)
            last.then_inc(S["evac_act"], 1)

        for n in range(NU + 3):
            if n < NU:
                i, br, h, kbs = units[n]
                act.wait_ge(S["front"], n + 1)
                if n >= 3:
                    act.wait_ge(S["t_done"], first_group[n - 2])
                nk = P * len(kbs)
                s0, v = 2 * (n % 2), n % 4
                if br == "A":
                    nc.scalar.activation(esk[:, v, :], esk[:, v, :], ACT.Exp)
                    for g in range(2):
                        last = nc.scalar.activation(PB[:, n % 3, nk * g:nk * g + nk], PS[:, s0, nk * g:nk * g + nk],
                                                    ACT.Exp, bias=ngm[:, v, g:g + 1], scale=SC,
                                                    accum_out=den[:, v, g:g + 1])
                elif br == "C":
                    last = nc.scalar.activation(pc[:, :, :], pc[:, :, :], ACT.Exp, scale=SC)
                else:
                    a = min(nk, 512)
                    src = PS[:, s0:s0 + 2, :].rearrange("p a n -> p (a n)")[:, 0:nk]
                    last = nc.scalar.activation(PB[:, n % 3, 0:nk], src, ACT.Exp, bias=ngm[:, v, 0:1], scale=SC,
                                                accum_out=den[:, v, 0:1])
                last.then_inc(S["exp_done"], 1)
            if 2 <= n < NU + 2:
                for m in range(first_group[n - 2], first_group[n - 1]):
                    if m % 2 == 0:
                        move_group(m)
            if n >= 3 and (n - 3) == last_of[units[n - 3][:2]]:
                i, br = units[n - 3][:2]
                if br in "AS":
                    act.wait_ge(S["pv_done"], pv_order.index((i, br)) + 1)
                    act.wait_ge(S["s_ready"], last_of[(i, br)] + 1)
                    dst = (qa if br == "A" else qb)[:, :, P * i:P * i + P]
                    nc.scalar.copy(dst, PS[:, 6 if br == "A" else 7, :].rearrange("p (r t) -> p r t", r=REP)) \
                        .then_inc(S["o_evac"], 1)

        for pi in range(2 * KT):
            act.wait_ge(S["gate_in"], pi + 1)
            if pi == 0:
                act.wait_ge(S["zero_done"], 16 * (MAXB + 1))
            if pi >= 2:
                act.wait_ge(S["merge_dve"], pi - 1)
            for j in range(2):
                last = nc.scalar.activation(tmp[:, pi % 2, j, :], PS[:, 4 * (pi % 2) + j, :], ACT.Tanh, scale=0.5)
            last.then_inc(S["gate_act"], 1)

        act.wait_ge(S["merge_ps"], 2 * KT)
        for i in range(TT + 1):
            if i < TT:
                act.wait_ge(S["h2_done"], i + 1)
                nc.scalar.activation(junk2[:, :], h2[:, i % 2, :], ACT.Square,
                                     accum_out=stat[:, 0, i:i + 1]).then_inc(S["act_step"], 1)
                act.wait_ge(S["act_step"], TT + i + 1)
                nc.scalar.activation(stat[:, 1, i:i + 1], stat[:, 0, i:i + 1], ACT.Sqrt, bias=eps_t[:, :],
                                     scale=1.0 / D).then_inc(S["h2_std"], 1)
            if i >= 1:
                m = i - 1
                act.wait_ge(S["h2T_ps"], m + 1)
                if m >= 2:
                    act.wait_ge(S["log_ps"], m - 1)
                nc.scalar.copy(h2T[:, m % 2, :, :].rearrange("p (a k) n -> p a (k n)", a=2), PS[:, 4:6, :]) \
                    .then_inc(S["h2T_done"], 1)

        act.wait_ge(S["route_arg"], 1)
        nc.scalar.activation(G4[4][:, :, :], G4[3][:, :, :], ACT.Exp)
        nc.scalar.activation(G8[5][:, :], G8[4][:, :], ACT.Exp).then_inc(S["route_exp"], 1)

        act.wait_ge(S["routed"], 1)
        total = act.value_load(starts_i[0:1, NE:NE + 1], min_val=NE, max_val=MAXB)
        act.wait_ge(S["x_tr"], 1)
        nc.scalar.copy(xT_out, xT_ps).then_inc(S["xT_evac"], 1)
        with act.Fori(0, total) as b:
            act.wait_ge(S["mm1"], b + 1)
            nc.scalar.activation(th[:, :], PS[:, 0, 0:256], ACT.Tanh, scale=0.5).then_inc(S["tanh_done"], 1)
            act.wait_ge(S["x_tr"], b + 2)
            act.wait_ge(S["mm3"], b + 1)
            nc.scalar.copy(xT_out, xT_ps).then_inc(S["xT_evac"], 1)
            act.wait_ge(S["y_ps"], b + 1)
            act.wait_ge(S["y_free"], b + 1)
            nc.scalar.copy(ysb[:, :], PS[:, 3, :]).then_inc(S["y_evac"], 1)

        for i in range(TT):
            act.wait_ge(S["comb_sum"], i + 1)
            nc.scalar.activation(fjunk[:, :], fin_h[:, i % 2, :], ACT.Square,
                                 accum_out=stat[:, 0, i:i + 1]).then_inc(S["act_step"], 1)
            act.wait_ge(S["act_step"], 2 * TT + i + 1)
            nc.scalar.activation(stat[:, 1, i:i + 1], stat[:, 0, i:i + 1], ACT.Sqrt, bias=eps_t[:, :],
                                 scale=1.0 / D).then_inc(S["comb_std"], 1)

    @block.vector
    def _(dve):
        steps = [0]

        def step(ins):
            steps[0] += 1
            ins.then_inc(S["dve_step"], 1)
            dve.wait_ge(S["dve_step"], steps[0])

        dve.wait_ge(S["small_in"], 16 * NSMALL)
        for i in range(TT + 1):
            if i < TT:
                dve.wait_ge(S["std_done"], i + 1)
                step(dve.reciprocal(stat[:, 2, i:i + 1], stat[:, 1, i:i + 1]))
                if i >= 2:
                    dve.wait_ge(S["xT_ps"], i - 1)
                dve.tensor_scalar(xs[:, i % 2, :], xt[:, i % 2, :], stat[:, 2, i:i + 1], None, ALU.mult) \
                    .then_inc(S["xs_ready"], 1)
            if i >= 1:
                m = i - 1
                dve.wait_ge(S["xT_ps"], m + 1)
                src = PS[:, 2 * (m % 2):2 * (m % 2) + 2, :].rearrange("p a (k n) -> p (a k) n", n=P)
                dve.tensor_tensor(hnT[:, :, P * m:P * m + P], src, gT[:, :].unsqueeze(2).to_broadcast([P, KT, P]),
                                  ALU.mult).then_inc(S["hnT_done"], 1)
        dve.tensor_scalar(nsink[:, :, :], sinks[:, :, :], -1.0, None, ALU.mult).then_inc(S["nsink_done"], 1)
        dve.wait_ge(S["bias_ps"], 1)
        for w in range(2):
            dve.tensor_tensor(tab_vec[:, w, :], PS[0:8, 4 + w, 0:RV], hmask[:, w, :], ALU.add).then_inc(S["bias_vec"], 1)

        def blocks_plus_pos(w):
            b = c2[:, w, 0, 0:1]
            src = bass.AP(b.tensor, b.offset, [list(b.ap[0]), [2, 16], [SEQ, 2], [16, NB]])
            dve.tensor_tensor(xblk[:, :, :, :], src, pos[:, w, :].unsqueeze(2).unsqueeze(3).to_broadcast([P, 16, 2, NB]),
                              ALU.add).then_inc(S["xblk_done"], 1)

        for j, (name, c, h) in enumerate(jobs):
            if j % 2 == 1:
                dve.wait_ge(S["proj_ps"], j + 1)
                for ins in evacuate(dve, name, c, h, j % 4, dve.tensor_copy):
                    last = ins
                last.then_inc(S["proj_dve"], 1)
            if j == 3:
                dve.wait_ge(S["proj_act"], 1)
                dve.wait_ge(S["proj_dve"], 1)
                blocks_plus_pos(0)
            if j == 13:
                dve.wait_ge(S["proj_act"], 2)
                dve.wait_ge(S["hid_ps"], 1)
                blocks_plus_pos(1)
            if j in (15, 29):
                w = 0 if j == 15 else 1
                hid = PS[:, 6 + w, 0:252]
                dve.wait_ge(S["hid_ps"], w + 1)
                step(dve.tensor_copy(gel[:, 2, :], hid))
                step(dve.tensor_tensor(gel[:, 0, :], gel[:, 2, :], gel[:, 2, :], ALU.mult))
                step(dve.tensor_scalar(gel[:, 0, :], gel[:, 0, :], 0.044715, 1.0, ALU.mult, ALU.add))
                dve.tensor_tensor(gel[:, 0, :], gel[:, 0, :], gel[:, 2, :], ALU.mult).then_inc(S["gelu_arg"], 1)
                dve.wait_ge(S["gelu_act"], w + 1)
                dve.scalar_tensor_tensor(gel[:, 2, :], gel[:, 1, :], 1.0, hid, ALU.add, ALU.mult) \
                    .then_inc(S["gelu_dve"], 1)
            if j == 21:
                dve.wait_ge(S["cmp_ps"], 1)
                dve.wait_ge(S["kz_zero"], 2)
                dve.tensor_scalar(kcz[0:DH, 0:NB], PS[0:DH, 4, 0:NB], 0.5, None, ALU.mult)
                dve.tensor_scalar(kcz[DH:P, DH:DH + NB], PS[0:DH, 4, NB:2 * NB], 0.5, None, ALU.mult) \
                    .then_inc(S["cmp_done"], 1)
        dve.wait_ge(S["cmp_ps"], 2)
        for g in range(2):
            last = dve.tensor_scalar(vcz[DH * g:DH * g + NB, DH * g:DH * g + DH], PS[0:NB, 5, DH * g:DH * g + DH],
                                     0.5, None, ALU.mult)
        last.then_inc(S["cmp_done"], 1)
        dve.wait_ge(S["tanh_gates"], 1)
        step(dve.tensor_scalar(gates[:, :, :], gates[:, :, :], 0.5, 0.5, ALU.mult, ALU.add))
        dve.wait_ge(S["bias_in"], 16)

        def front(n):
            i, br, h, kbs = units[n]
            dve.wait_ge(S["s_ready"], n + 1)
            nk, s0, v = P * len(kbs), 2 * (n % 2), n % 4
            if br == "A":
                s = PS[:, s0, 0:2 * nk].rearrange("p (g k) -> p g k", g=2)
                bb = bias[:, 0:8, :].rearrange("p (g r) k -> p g r k", g=2)[:, :, h, 256 - nk:256]
                step(dve.tensor_tensor(s, s, bb, ALU.add))
                step(dve.tensor_reduce(mx[:, v, 0:2], s, X, ALU.max))
                step(dve.scalar_tensor_tensor(ngm[:, v, :], mx[:, v, 0:2], -SC, nsink[:, :, h], ALU.mult, ALU.min))
                dve.tensor_tensor(esk[:, v, :], ngm[:, v, :], sinks[:, :, h], ALU.add).then_inc(S["front"], 1)
            elif br == "C":
                s = PS[:, s0, :].rearrange("p (h k) -> p h k", h=8)
                step(dve.tensor_tensor(s, s, cmpmask[:, i, :].unsqueeze(1).to_broadcast([P, 8, 64]), ALU.add))
                step(dve.tensor_reduce(mx[:, v, :], s, X, ALU.max))
                if i >= 1:
                    dve.wait_ge(S["t_done"], first_group[last_of[(i - 1, "C")] + 1])
                dve.tensor_tensor(pc[:, :, :], s, mx[:, v, :].unsqueeze(2).to_broadcast([P, 8, 64]), ALU.subtract) \
                    .then_inc(S["front"], 1)
            else:
                s = PS[:, s0:s0 + 2, :].rearrange("p a n -> p (a n)")
                near = min(nk, 256)
                ins = dve.tensor_tensor(s[:, nk - near:nk], s[:, nk - near:nk], bias[:, 8 + h, 256 - near:256], ALU.add)
                if br == "W" and i >= WIN_BLOCKS:
                    ins = dve.tensor_tensor(s[:, 0:P], s[:, 0:P], winmask[:, :], ALU.add)
                step(ins)
                step(dve.tensor_reduce(mx[:, v, 0:1], s[:, 0:nk], X, ALU.max))
                dve.tensor_scalar(ngm[:, v, 0:1], mx[:, v, 0:1], -SC, None, ALU.mult).then_inc(S["front"], 1)

        def back(n):
            i, br, h, kbs = units[n]
            v = n % 4
            dve.wait_ge(S["exp_done"], n + 1)
            if br == "A":
                step(dve.tensor_tensor(den[:, v, 0:2], den[:, v, 0:2], esk[:, v, :], ALU.add))
                dve.reciprocal(rin[:, v, 0:2], den[:, v, 0:2]).then_inc(S["back"], 1)
            elif br == "C":
                step(dve.tensor_reduce(den[:, v, :], pc[:, :, :], X, ALU.add))
                step(dve.reciprocal(rin[:, v, :], den[:, v, :]))
                ga = gates[:, i, :].rearrange("p (g r j) -> p r g j", g=2, r=REP)[:, :, :, 0]
                ri = rin[:, v, :].rearrange("p (r g) -> p r g", g=2)
                ins = dve.tensor_tensor(ri, ri, ga, ALU.mult)
                if i == 0:
                    step(ins)
                    ins = dve.tensor_scalar(rin[:, v, :], rin[:, v, :], rowok[:, 0:1], None, ALU.mult)
                ins.then_inc(S["back"], 1)
            else:
                dve.reciprocal(rin[:, v, 0:1], den[:, v, 0:1]).then_inc(S["back"], 1)

        for n in range(NU + 2):
            if n < NU:
                front(n)
            if 1 <= n < NU + 1:
                back(n - 1)
            if n >= 2:
                for m in range(first_group[n - 2], first_group[n - 1]):
                    if m % 2 == 1:
                        dve.wait_ge(S["t_done"], m + 1)
                        slot_free(dve, m)
                        for dst, src in group_copies(m):
                            last = dve.tensor_copy(dst, src)
                        last.then_inc(S["evac_dve"], 1)

        dve.wait_ge(S["zero_done"], 16 * (MAXB + 1))
        for pi in range(2 * KT):
            b0, m = 4 * (pi % 2), pi % 2
            dve.wait_ge(S["gate_act"], pi + 1)
            dve.wait_ge(S["merge_ps"], pi + 1)
            for j in range(2):
                ins = dve.scalar_tensor_tensor(tmp[:, m, 2 + j, :], tmp[:, m, j, :], 1.0, PS[:, b0 + 2 + j, :],
                                               ALU.add, ALU.mult)
            step(ins)
            dt, hf = pi // 2, pi % 2
            dst = mT[:, 4 * hf:4 * hf + 4, dt, :]
            dve.tensor_tensor(dst, tmp[:, m, 2, :].rearrange("p (t n) -> p t n", n=P),
                              tmp[:, m, 3, :].rearrange("p (t n) -> p t n", n=P), ALU.add).then_inc(S["merge_dve"], 1)

        def logits(m):
            dve.wait_ge(S["log_ps"], m + 1)
            dve.tensor_tensor(lgs[:, m, :], PS[:, 6, 0:36], rbias[:, :], ALU.add).then_inc(S["log_done"], 1)

        dve.wait_ge(S["gff_in"], 16)
        dve.wait_ge(S["wr_in"], 64)
        for i in range(TT + 1):
            if i < TT:
                dve.wait_ge(S["out_ps"], i + 1)
                dve.wait_ge(S[f"xr_in{i % 2}"], 16 * (i // 2 + 1))
                if i >= 2:
                    dve.wait_ge(S[f"h2_st{i % 2}"], 16 * (i // 2))
                    dve.wait_ge(S["hn2_done"], i - 1)
                src = PS[:, 2 * (i % 2):2 * (i % 2) + 2, :].rearrange("p a n -> p (a n)")
                dve.scalar_tensor_tensor(h2[:, i % 2, :], src, 0.5, xr[:, i % 2, :], ALU.mult, ALU.add) \
                    .then_inc(S["h2_done"], 1)
                dve.wait_ge(S["h2_std"], i + 1)
                dve.wait_ge(S["h2_done"], i + 1)
                step(dve.reciprocal(stat[:, 2, i:i + 1], stat[:, 1, i:i + 1]))
                dve.scalar_tensor_tensor(mT[:, i, :, :].rearrange("p k n -> p (k n)"), h2[:, i % 2, :],
                                         stat[:, 2, i:i + 1], gff[:, :], ALU.mult, ALU.mult).then_inc(S["hn2_done"], 1)
            if i >= 1:
                logits(i - 1)

        def first_of_max(src, scores_out, best, rev, a, b, c):
            n = rev.shape[-1]
            step(dve.tensor_reduce(best, src, X, ALU.max))
            step(dve.tensor_tensor(a, src, best.unsqueeze(2).to_broadcast([P, TT, n]), ALU.is_equal))
            step(dve.tensor_tensor(b, a, rev.unsqueeze(1).to_broadcast([P, TT, n]), ALU.mult))
            step(dve.tensor_reduce(c, b, X, ALU.max))
            step(dve.tensor_tensor(scores_out, b, c.unsqueeze(2).to_broadcast([P, TT, n]), ALU.is_equal))

        dve.wait_ge(S["tables"], 1)
        dve.wait_ge(S["log_done"], TT)
        L4, LE = lgs[:, :, 0:NG], lgs[:, :, NG:NG + NE]
        first_of_max(L4, G4[2][:, :, :], G8[0], rev4, G4[0][:, :, :], G4[1][:, :, :], G8[1])
        step(dve.tensor_tensor(G4[3][:, :, :], L4, G8[0].unsqueeze(2).to_broadcast([P, TT, NG]), ALU.subtract))
        step(dve.tensor_scalar(G4[0][:, :, :], G4[2][:, :, :], -NEG, NEG, ALU.mult, ALU.add))
        step(dve.tensor_tensor(G32[0].rearrange("p t (g e) -> p t g e", g=NG), LE.rearrange("p t (g e) -> p t g e", g=NG),
                               G4[0][:, :, :].unsqueeze(3).to_broadcast([P, TT, NG, EPG]), ALU.add))
        first_of_max(G32[0], onehot[0], G8[2], rev32, G32[1], G32[2], G8[1])
        step(dve.scalar_tensor_tensor(G32[3], onehot[0], 2 * NEG, G32[0], ALU.mult, ALU.add))
        first_of_max(G32[3], onehot[1], G8[3], rev32, G32[1], G32[2], G8[1])
        dve.tensor_tensor(assign[:, :].rearrange("p (t n) -> p t n", t=TT), onehot[0], onehot[1], ALU.add) \
            .then_inc(S["assigned"], 1)
        dve.tensor_tensor(G8[4], G8[3], G8[2], ALU.subtract).then_inc(S["route_arg"], 1)
        dve.wait_ge(S["route_exp"], 1)
        step(dve.tensor_reduce(G8[6], G4[4][:, :, :], X, ALU.add))
        step(dve.scalar_tensor_tensor(G8[7], G8[5], 1.0, G8[6], ALU.add, ALU.mult))
        step(dve.reciprocal(tokw[:, 0, :], G8[7]))
        step(dve.tensor_tensor(tokw[:, 1, :], tokw[:, 0, :], G8[5], ALU.mult))
        dve.wait_ge(S["route_ps"], 1)
        tot = PS[:, 1, 0:256].rearrange("p (t n) -> p t n", t=TT)
        step(dve.memset(offs[:, 0, :], 0.0))
        for i in range(1, TT):
            step(dve.tensor_tensor(offs[:, i, :], offs[:, i - 1, :], tot[:, i - 1, :], ALU.add))
        step(dve.tensor_tensor(cnt, offs[:, TT - 1, :], tot[:, TT - 1, :], ALU.add))
        b15 = big.rearrange("p e f -> p (e f)")[:, 0:NE * 15].rearrange("p (e f) -> p e f", e=NE)
        step(dve.tensor_tensor(b15, cnt.unsqueeze(2).to_broadcast([P, NE, 15]), lim.unsqueeze(1).to_broadcast([P, NE, 15]),
                               ALU.is_gt))
        step(dve.tensor_reduce(nblk, b15, X, ALU.add))
        step(dve.tensor_scalar(nblk, nblk, 1.0, None, ALU.add))
        step(dve.tensor_tensor(big, nblk.unsqueeze(1).to_broadcast([P, NE, NE]), upto, ALU.mult))
        step(dve.memset(starts_f[:, 0:1], 0.0))
        step(dve.tensor_reduce(starts_f[:, 1:NE + 1], big, X, ALU.add))
        step(dve.tensor_copy(starts_i[:, :], starts_f[:, :]))
        step(dve.tensor_scalar(base32, starts_f[:, 0:NE], float(SLOTS), None, ALU.mult))
        step(dve.tensor_tensor(offs[:, :, :], offs[:, :, :], base32.unsqueeze(1).to_broadcast([P, TT, NE]), ALU.add))
        step(dve.tensor_tensor(offs[:, :, :], offs[:, :, :], PS[:, 0, 0:256].rearrange("p (t n) -> p t n", t=TT), ALU.add))
        for c in range(2):
            step(dve.tensor_tensor(G32[1], onehot[c], offs[:, :, :], ALU.mult))
            step(dve.tensor_reduce(G8[8 + c], G32[1], X, ALU.add))
            step(dve.tensor_copy(slots_i[:, c, :], G8[8 + c]))
        dve.sem_inc(S["routed"], 1)

        total = dve.value_load(starts_i[0:1, NE:NE + 1], min_val=NE, max_val=MAXB)
        with dve.Fori(0, total) as b:
            dve.wait_ge(S["tanh_done"], b + 1)
            dve.scalar_tensor_tensor(hu[:, :], th[:, :], 1.0, PS[:, 0, 0:256], ALU.add, ALU.mult).then_inc(S["hu_done"], 1)
            dve.wait_ge(S["hu_done"], b + 1)
            dve.wait_ge(S["mm3"], b + 1)
            dve.scalar_tensor_tensor(hv[:, :], hu[:, :], 0.5, PS[:, 1, 0:256], ALU.mult, ALU.mult) \
                .then_inc(S["hid_done"], 1)
            dve.wait_ge(S["hT_ps"], b + 1)
            dve.tensor_copy(hT[:, :, :].rearrange("p j n -> p (j n)"), PS[:, 2, 0:256]).then_inc(S["hT_done"], 1)

        dve.wait_ge(S["gfin_in"], 16)
        for i in range(TT):
            m = i % 2
            dve.wait_ge(S[f"xr_in{m}"], 16 * (TT // 2 + i // 2 + 1))
            dve.wait_ge(S[f"g_in{m}"], 32 * (i // 2 + 1))
            step(dve.scalar_tensor_tensor(fin_h[:, m, :], fin_y[:, m, 0, :], tokw[:, 0, i:i + 1], fin_h[:, m, :],
                                          ALU.mult, ALU.add))
            dve.scalar_tensor_tensor(fin_h[:, m, :], fin_y[:, m, 1, :], tokw[:, 1, i:i + 1], fin_h[:, m, :],
                                     ALU.mult, ALU.add).then_inc(S["comb_sum"], 1)
            dve.wait_ge(S["comb_std"], i + 1)
            step(dve.reciprocal(stat[:, 2, i:i + 1], stat[:, 1, i:i + 1]))
            if i >= 2:
                dve.wait_ge(S[f"out_st{m}"], 16 * (i // 2))
            dve.scalar_tensor_tensor(fin_o[:, m, :], fin_h[:, m, :], stat[:, 2, i:i + 1], gfin[:, :],
                                     ALU.mult, ALU.mult).then_inc(S["comb_done"], 1)

    @block.gpsimd
    def _(pool):
        steps = [0]

        def step(ins):
            steps[0] += 1
            ins.then_inc(S["pool_step"], 1)
            pool.wait_ge(S["pool_step"], steps[0])

        g = nc.gpsimd
        step(g.memset(ident[:, :], 0.0))
        step(g.memset(eps_t[:, :], EPS))
        step(g.memset(ones[:, :], 1.0))
        step(g.memset(tri[:, :], 1.0))
        step(g.memset(winmask[:, :], 0.0))
        step(g.memset(rowok[:, :], 1.0))
        step(g.memset(cmpmask[:, :, :], 0.0))
        step(g.affine_select(out=ident[:, :], in_=ident[:, :], compare_op=ALU.not_equal, fill=1.0, base=0,
                             pattern=[[-1, P]], channel_multiplier=1))
        pool.sem_inc(S["const_ready"], 1)
        step(g.memset(kcz[:, :], 0.0))
        step(g.memset(vcz[:, :], 0.0))
        g.memset(kz[DH:P, :, 0, :], 0.0).then_inc(S["kz_zero"], 1)
        pool.wait_ge(S["kz_zero"], 1)
        g.memset(kz[0:DH, :, 1, :], 0.0).then_inc(S["kz_zero"], 1)
        pool.wait_ge(S["kz_zero"], 2)
        step(g.affine_select(out=tri[:, :], in_=tri[:, :], compare_op=ALU.is_gt, fill=0.0, base=0,
                        pattern=[[1, P]], channel_multiplier=-1))
        step(g.affine_select(out=winmask[:, :], in_=winmask[:, :], compare_op=ALU.is_gt, fill=8 * NEG, base=0,
                        pattern=[[1, P]], channel_multiplier=-1))
        step(g.affine_select(out=rowok[:, :], in_=rowok[:, :], compare_op=ALU.is_ge, fill=0.0, base=-31,
                        pattern=[[0, 1]], channel_multiplier=1))
        g.affine_select(out=cmpmask[:, :, :], in_=cmpmask[:, :, :], compare_op=ALU.is_ge, fill=8 * NEG, base=-31,
                        pattern=[[P, TT], [-16, 64]], channel_multiplier=1).then_inc(S["masks_ready"], 1)

        for n, (i, br, h, kbs) in enumerate(units):
            nk, v = P * len(kbs), n % 4
            pool.wait_ge(S["back"], n + 1)
            if br == "A":
                for gg in range(2):
                    pr = PB[:, n % 3, nk * gg:nk * gg + nk]
                    last = g.tensor_scalar(pr, pr, rin[:, v, gg:gg + 1], None, ALU.mult)
            elif br == "C":
                last = g.tensor_tensor(pc[:, :, :], pc[:, :, :], rin[:, v, :].unsqueeze(2).to_broadcast([P, 8, 64]), ALU.mult)
            else:
                col = 3 * h + (1 if br == "S" else 2)
                pr = PB[:, n % 3, 0:nk]
                last = g.tensor_scalar(pr, pr, rin[:, v, 0:1], gates[:, i, col:col + 1], ALU.mult, ALU.mult)
            last.then_inc(S["scaled"], 1)

        pool.wait_ge(S["scaled"], NU)
        pool.wait_ge(S["t_done"], len(groups))
        pool.wait_ge(S["merge_ps"], 2 * KT)
        step(g.memset(wr[:, :, :], 0.0))
        pool.dma_start(wr[:, :, 0:NG], t["w_group"].rearrange("(k p) n -> p k n", p=P)).then_inc(S["wr_in"], 16)
        pool.dma_start(wr[:, :, NG:NG + NE], t["w_expert"].rearrange("(k p) n -> p k n", p=P)).then_inc(S["wr_in"], 16)
        pool.dma_start(rbias[:, 0:NG], t["b_group"].partition_broadcast(P)).then_inc(S["wr_in"], 16)
        pool.dma_start(rbias[:, NG:NG + NE], t["b_expert"].partition_broadcast(P)).then_inc(S["wr_in"], 16)

        pool.wait_ge(S["out_ps"], TT)
        step(g.iota(rev4, [[-1, NG]], base=NG, channel_multiplier=0, allow_small_or_imprecise_dtypes=True))
        step(g.iota(rev32, [[-1, NE]], base=NE, channel_multiplier=0, allow_small_or_imprecise_dtypes=True))
        step(g.iota(lim, [[SLOTS, 15]], base=SLOTS, channel_multiplier=0, allow_small_or_imprecise_dtypes=True))
        step(g.memset(upto, 1.0))
        g.affine_select(out=upto, in_=upto, compare_op=ALU.is_ge, fill=0.0, base=0,
                        pattern=[[1, NE], [-1, NE]], channel_multiplier=0).then_inc(S["tables"], 1)

        pool.wait_ge(S["routed"], 1)
        pool.wait_ge(S["zero_done"], 16 * (MAXB + 1))
        pool.wait_ge(S["hn2_done"], TT)
        for i in range(TT):
            for c in range(2):
                g.indirect_dma_start(rows_d[0:MAXB * SLOTS, :], bass.IndirectOffsetOnAxis(ap=slots_i[:, c, i:i + 1], axis=0),
                                     mT[:, i, :, :].rearrange("p k n -> p (k n)"), None).then_inc(S["scattered"], 16)
        pool.wait_ge(S["scattered"], 16 * 2 * TT)

        total = pool.value_load(starts_i[0:1, NE:NE + 1], min_val=NE, max_val=MAXB)
        for n in range(2):
            pool.dma_start(xin[SLOTS * n:SLOTS * n + SLOTS, :], rows_d[0:SLOTS, 512 * n:512 * n + 512]).then_inc(S["x_blk"], 16)
        pool.sem_inc(S["y_free"], 1)
        with pool.Fori(0, total) as b:
            pool.wait_ge(S["x_tr"], b + 1)
            for n in range(2):
                pool.dma_start(xin[SLOTS * n:SLOTS * n + SLOTS, :],
                               rows_d[bass.ds(b * SLOTS + SLOTS, SLOTS), 512 * n:512 * n + 512]).then_inc(S["x_blk"], 16)
            pool.wait_ge(S["y_evac"], b + 1)
            for n in range(2):
                pool.dma_start(rows_d[bass.ds(b * SLOTS, SLOTS), 512 * n:512 * n + 512],
                               ysb[DH * n:DH * n + DH, :]).then_inc(S["y_st"], 16)
            pool.wait_ge(S["y_st"], b * 32 + 32)
            pool.sem_inc(S["y_free"], 1)
        pool.sem_inc(S["loop_left"], 1)

        pool.dma_start(gfin[:, :], t["norm_final"].partition_broadcast(P)).then_inc(S["gfin_in"], 16)
        for i in range(TT):
            if i >= 2:
                pool.wait_ge(S["comb_sum"], i - 1)
            for c in range(2):
                g.indirect_dma_start(fin_y[:, i % 2, c, :], None, rows_d[0:MAXB * SLOTS, :],
                                     bass.IndirectOffsetOnAxis(ap=slots_i[:, c, i:i + 1], axis=0)).then_inc(S[f"g_in{i % 2}"], 16)

    ctx.close()


INPUTS = ["x", "rel_bias", "norm_mix", "w_in", "a_sinks", "cmp_pos_k", "cmp_w1_k", "cmp_w2_k", "cmp_pos_v", "cmp_w1_v",
          "cmp_w2_v", "w_br_a", "w_br_b", "w_out", "norm_ffn", "w_group", "b_group", "w_expert", "b_expert", "w1", "w3",
          "w2", "norm_final"]
STACKED = [n for n in INPUTS if n not in ("x", "rel_bias", "norm_final")]


def kernel(**inputs):
    import concourse.bacc as bacc
    from concourse.bass_utils import run_bass_kernel_spmd

    nc = bacc.Bacc("TRN2", target_bir_lowering=False, num_devices=1)
    hot, mask = shape_constants()
    arrays = {n: np.ascontiguousarray(inputs[n]) for n in INPUTS}
    arrays.update(bucket_hot=hot, distance_mask=mask)
    t = {}
    for n, a in arrays.items():
        ap = nc.dram_tensor(n, a.shape, mybir.dt.from_np(a.dtype), kind="ExternalInput").ap()
        t[n] = ap[0] if n in STACKED else ap
    out = nc.dram_tensor("out", (1, SEQ, D), F32, kind="ExternalOutput").ap()
    build(nc, t, out)
    r = run_bass_kernel_spmd(nc, [arrays], core_ids=[0])
    return r.results[0]["out"]
```
